# Optimizing a Trainium2 kernel written in Bass

```python
import math
import jax, jax.numpy as jnp
from jax import lax
import numpy as np

D_MODEL = 1024
BATCH = 1
SEQ = 256
DEPTH = 2

EPS = 1e-6
ATT_HEAD_DIM = 64
ATT_WIDTH = D_MODEL // 2
ATT_HEADS = ATT_WIDTH // ATT_HEAD_DIM
Q_BLOCK = 128
POOL_WIDTH = D_MODEL // 4
POOL_WINDOWS = (2, 4, 8, 16)
POOL_GROUPS = len(POOL_WINDOWS)
POOL_GROUP_DIM = POOL_WIDTH // POOL_GROUPS
SSM_WIDTH = D_MODEL - ATT_WIDTH - POOL_WIDTH
SSM_GROUP_CH = 16
SSM_GROUPS = SSM_WIDTH // SSM_GROUP_CH
SSM_STATE = 64
IN_COLS = 3 * ATT_WIDTH + ATT_HEADS + POOL_WIDTH + SSM_WIDTH
IN_SPLITS = (ATT_WIDTH, 2 * ATT_WIDTH, 3 * ATT_WIDTH, 3 * ATT_WIDTH + ATT_HEADS,
             3 * ATT_WIDTH + ATT_HEADS + POOL_WIDTH)
PEER_HEADS = 8
PEER_KEYS = 128
PEER_EXPERTS = PEER_KEYS * PEER_KEYS
PEER_QDIM = 256
PEER_HALF = PEER_QDIM // 2
PEER_TOPK = 16
PEER_CHUNK = 128

kernel_name = 'hybrid_fox_pool_s5_peer'

def rms_norm(x, g):
    xf = x.astype(jnp.float32)
    y = xf * lax.rsqrt(jnp.mean(xf * xf, axis=-1, keepdims=True) + EPS)
    return (y * g.astype(jnp.float32)).astype(x.dtype)

def forgetting_attention(q, k, v, f_logit, q_gain, k_gain):
    b, s, h, dh = q.shape
    qf = rms_norm(q, q_gain).astype(jnp.float32) * (dh ** -0.5)
    kf = rms_norm(k, k_gain).astype(jnp.float32)
    vf = v.astype(jnp.float32)
    c_t = jnp.cumsum(jax.nn.log_sigmoid(f_logit.astype(jnp.float32)), axis=1).transpose(0, 2, 1)
    nb = s // Q_BLOCK
    q_blocks = qf.reshape(b, nb, Q_BLOCK, h, dh).transpose(1, 0, 2, 3, 4)
    c_blocks = c_t.reshape(b, h, nb, Q_BLOCK).transpose(2, 0, 1, 3)
    key_pos = jnp.arange(s)

    def block(args):
        i, q_i, c_i = args
        logits = jnp.einsum('bqhd,bkhd->bhqk', q_i, kf) + c_i[..., :, None] - c_t[:, :, None, :]
        q_pos = i * Q_BLOCK + jnp.arange(Q_BLOCK)
        causal = key_pos[None, :] <= q_pos[:, None]
        p = jax.nn.softmax(jnp.where(causal, logits, -jnp.inf), axis=-1)
        return jnp.einsum('bhqk,bkhd->bqhd', p, vf)

    out = lax.map(block, (jnp.arange(nb), q_blocks, c_blocks))
    return out.transpose(1, 0, 2, 3, 4).reshape(b, s, h * dh).astype(v.dtype)

def multiscale_pool(u, pool_w, pool_scale):
    b, s, _ = u.shape
    uf = u.astype(jnp.float32).reshape(b, s, POOL_GROUPS, POOL_GROUP_DIM)
    cs = jnp.pad(jnp.cumsum(uf, axis=1), ((0, 0), (1, 0), (0, 0), (0, 0)))
    pos = jnp.arange(s)
    means = []
    for g, w in enumerate(POOL_WINDOWS):
        lo = jnp.maximum(pos + 1 - w, 0)
        cnt = (pos + 1 - lo).astype(jnp.float32)[None, :, None]
        means.append((cs[:, pos + 1, g] - cs[:, lo, g]) / cnt)
    pooled = jnp.stack(means, axis=2) - uf
    mixed = jnp.einsum('bsgc,gcd->bsgd', pooled, pool_w.astype(jnp.float32)).reshape(b, s, POOL_WIDTH)
    return (mixed * pool_scale.astype(jnp.float32)).astype(u.dtype)

def s5_mixer(u, a_re, a_im, log_dt, b_re, b_im, c_re, c_im, d_skip, glu_w, glu_b):
    bsz, s, _ = u.shape
    uf = u.astype(jnp.float32).reshape(bsz, s, SSM_GROUPS, SSM_GROUP_CH)
    a = lax.complex(a_re.astype(jnp.float32), a_im.astype(jnp.float32))
    dt = jnp.exp(log_dt.astype(jnp.float32))[:, None]
    a_bar = jnp.exp(a * dt)
    b_mat = lax.complex(b_re.astype(jnp.float32), b_im.astype(jnp.float32))
    b_bar = ((a_bar - 1.0) / a)[..., None] * b_mat
    bu = jnp.einsum('bsgc,gpc->bsgp', uf.astype(jnp.complex64), b_bar)
    a_full = jnp.broadcast_to(a_bar, bu.shape)

    def combine(left, right):
        a_l, x_l = left
        a_r, x_r = right
        return a_l * a_r, a_r * x_l + x_r

    _, states = lax.associative_scan(combine, (a_full, bu), axis=1)
    c_mat = lax.complex(c_re.astype(jnp.float32), c_im.astype(jnp.float32))
    y = jnp.real(jnp.einsum('bsgp,gcp->bsgc', states, c_mat))
    y = y + d_skip.astype(jnp.float32).reshape(SSM_GROUPS, SSM_GROUP_CH) * uf
    z = jax.nn.gelu(y.reshape(bsz, s, SSM_WIDTH))
    out = z * jax.nn.sigmoid(z @ glu_w.astype(jnp.float32) + glu_b.astype(jnp.float32))
    return out.astype(u.dtype)

def mixer_sublayer(x, norm_g, w_in, f_bias, q_gain, k_gain, pool_w, pool_scale,
                   a_re, a_im, log_dt, b_re, b_im, c_re, c_im, d_skip, glu_w, glu_b,
                   out_norm_g, w_out):
    b, s, _ = x.shape
    h = rms_norm(x, norm_g)
    proj = jnp.einsum('bsd,de->bse', h, w_in)
    q, k, v, f_logit, u_pool, u_ssm = jnp.split(proj, IN_SPLITS, axis=-1)
    shp = (b, s, ATT_HEADS, ATT_HEAD_DIM)
    att = forgetting_attention(q.reshape(shp), k.reshape(shp), v.reshape(shp),
                               f_logit + f_bias, q_gain, k_gain)
    pool = multiscale_pool(u_pool, pool_w, pool_scale)
    ssm = s5_mixer(u_ssm, a_re, a_im, log_dt, b_re, b_im, c_re, c_im, d_skip, glu_w, glu_b)
    p0 = ATT_WIDTH
    p1 = ATT_WIDTH + POOL_WIDTH
    merged = jnp.concatenate([rms_norm(att, out_norm_g[:p0]),
                              rms_norm(pool, out_norm_g[p0:p1]),
                              rms_norm(ssm, out_norm_g[p1:])], axis=-1)
    return x + jnp.einsum('bse,ed->bsd', merged, w_out)

def peer_ffn(h, w_q, sub_keys, u_tab, v_tab):
    bsz, s, d = h.shape
    q = jnp.einsum('bsd,de->bse', h, w_q).astype(jnp.float32).reshape(bsz, s, PEER_HEADS, 2, PEER_HALF)
    scores = jnp.einsum('bshid,hikd->bshik', q, sub_keys.astype(jnp.float32))
    top_s, top_i = lax.top_k(scores, PEER_TOPK)
    cand = (top_s[..., 0, :, None] + top_s[..., 1, None, :]).reshape(bsz, s, PEER_HEADS, PEER_TOPK * PEER_TOPK)
    best_s, best_j = lax.top_k(cand, PEER_TOPK)
    i1 = jnp.take_along_axis(top_i[..., 0, :], best_j // PEER_TOPK, axis=-1)
    i2 = jnp.take_along_axis(top_i[..., 1, :], best_j % PEER_TOPK, axis=-1)
    experts = i1 * PEER_KEYS + i2
    gates = jax.nn.softmax(best_s, axis=-1)
    n_chunks = (bsz * s) // PEER_CHUNK
    hk = PEER_HEADS * PEER_TOPK
    h_c = h.astype(jnp.float32).reshape(n_chunks, PEER_CHUNK, d)
    e_c = experts.reshape(n_chunks, PEER_CHUNK, hk)
    g_c = gates.reshape(n_chunks, PEER_CHUNK, hk)

    def chunk(args):
        hh, ee, gg = args
        u_sel = u_tab[ee].astype(jnp.float32)
        v_sel = v_tab[ee].astype(jnp.float32)
        act = jax.nn.gelu(jnp.einsum('td,tkd->tk', hh, u_sel))
        return jnp.einsum('tk,tkd->td', gg * act, v_sel)

    out = lax.map(chunk, (h_c, e_c, g_c))
    return out.reshape(bsz, s, d).astype(h.dtype)

def setup_inputs(seed: int = 0) -> dict:
    key = jax.random.key(seed)
    ks = jax.random.split(key, 26)
    L, D = DEPTH, D_MODEL
    f32 = jnp.float32

    def nrm(k, shape, scale):
        return jax.random.normal(k, shape, f32) * scale

    def gain(k, shape):
        return 1.0 + 0.05 * jax.random.normal(k, shape, f32)

    n_idx = jnp.arange(SSM_STATE, dtype=f32)
    return {
        'x': nrm(ks[0], (BATCH, SEQ, D), 1.0),
        'norm1_g': gain(ks[1], (L, D)),
        'w_in': nrm(ks[2], (L, D, IN_COLS), D ** -0.5),
        'f_bias': jax.random.uniform(ks[3], (L, ATT_HEADS), f32, 1.0, 5.0),
        'q_gain': gain(ks[4], (L, ATT_HEAD_DIM)),
        'k_gain': gain(ks[5], (L, ATT_HEAD_DIM)),
        'pool_w': nrm(ks[6], (L, POOL_GROUPS, POOL_GROUP_DIM, POOL_GROUP_DIM), POOL_GROUP_DIM ** -0.5),
        'pool_scale': gain(ks[7], (L, POOL_WIDTH)),
        'ssm_a_re': -0.5 + 0.01 * jax.random.normal(ks[8], (L, SSM_GROUPS, SSM_STATE), f32),
        'ssm_a_im': math.pi * n_idx + 0.01 * jax.random.normal(ks[9], (L, SSM_GROUPS, SSM_STATE), f32),
        'ssm_log_dt': jax.random.uniform(ks[10], (L, SSM_GROUPS), f32, math.log(1e-3), math.log(1e-1)),
        'ssm_b_re': nrm(ks[11], (L, SSM_GROUPS, SSM_STATE, SSM_GROUP_CH), (2 * SSM_GROUP_CH) ** -0.5),
        'ssm_b_im': nrm(ks[12], (L, SSM_GROUPS, SSM_STATE, SSM_GROUP_CH), (2 * SSM_GROUP_CH) ** -0.5),
        'ssm_c_re': nrm(ks[13], (L, SSM_GROUPS, SSM_GROUP_CH, SSM_STATE), 0.5),
        'ssm_c_im': nrm(ks[14], (L, SSM_GROUPS, SSM_GROUP_CH, SSM_STATE), 0.5),
        'ssm_d': gain(ks[15], (L, SSM_WIDTH)),
        'glu_w': nrm(ks[16], (L, SSM_WIDTH, SSM_WIDTH), SSM_WIDTH ** -0.5),
        'glu_b': nrm(ks[17], (L, SSM_WIDTH), 0.01),
        'out_norm_g': gain(ks[18], (L, D)),
        'w_out': nrm(ks[19], (L, D, D), D ** -0.5),
        'norm2_g': gain(ks[20], (L, D)),
        'peer_wq': nrm(ks[21], (L, D, PEER_HEADS * PEER_QDIM), D ** -0.5),
        'peer_keys': nrm(ks[22], (L, PEER_HEADS, 2, PEER_KEYS, PEER_HALF), PEER_HALF ** -0.5),
        'peer_u': nrm(ks[23], (L, PEER_EXPERTS, D), D ** -0.5),
        'peer_v': nrm(ks[24], (L, PEER_EXPERTS, D), PEER_HEADS ** -0.5),
    }

def reference(x, norm1_g, w_in, f_bias, q_gain, k_gain, pool_w, pool_scale,
              ssm_a_re, ssm_a_im, ssm_log_dt, ssm_b_re, ssm_b_im, ssm_c_re, ssm_c_im,
              ssm_d, glu_w, glu_b, out_norm_g, w_out, norm2_g,
              peer_wq, peer_keys, peer_u, peer_v):
    for l in range(DEPTH):
        x = mixer_sublayer(x, norm1_g[l], w_in[l], f_bias[l], q_gain[l], k_gain[l],
                           pool_w[l], pool_scale[l], ssm_a_re[l], ssm_a_im[l], ssm_log_dt[l],
                           ssm_b_re[l], ssm_b_im[l], ssm_c_re[l], ssm_c_im[l], ssm_d[l],
                           glu_w[l], glu_b[l], out_norm_g[l], w_out[l])
        x = x + peer_ffn(rms_norm(x, norm2_g[l]), peer_wq[l], peer_keys[l], peer_u[l], peer_v[l])
    return x


_drawn_inputs = setup_inputs


def setup_inputs(seed=0):
    import zlib

    import numpy as np

    out = dict(_drawn_inputs(seed))
    spreads = {}
    factors = {'ssm_a_re': 6.416, 'glu_b': 5.617}
    for name, (base, spread) in spreads.items():
        noise = np.random.default_rng([zlib.crc32(name.encode()), seed]).standard_normal(out[name].shape)
        drawn = base * np.exp(spread * noise) if base else spread * noise
        out[name] = __import__('jax').numpy.asarray(drawn.astype(out[name].dtype))
    for name, factor in factors.items():
        out[name] = (out[name] * factor).astype(out[name].dtype)
    return out
```

```python
from contextlib import ExitStack

import numpy as np

import concourse.bass as bass
from concourse import mybir

F32 = mybir.dt.float32
U32 = mybir.dt.uint32
ALU = mybir.AluOpType
ACT = mybir.ActivationFunctionType
AX = mybir.AxisListType

P = 128
D = 1024
KD = D // P
SEQ = 256
TILES = SEQ // P
DEPTH = 2
STEPS = DEPTH * TILES
EPS = 1e-6
HEADS, DH = 8, 64
PAIRS = HEADS // 2
WINDOWS = (2, 4, 8, 16)
GROUPS, STATE, GCH = 16, 64, 16
SB = GROUPS * STATE // P
BCH = 2 * GCH
PH, KEYS, TOPK = 8, 128, 16
EXPERTS = KEYS * KEYS
PICKS = PH * TOPK
SLOTS = 12
GRP = 4
QUADS = PICKS // GRP
DIAGS = 6
NEG = -1.0e30
REPLACED = -3.0e38
HALVINGS = 9
TERMS = 5
GELU_C, GELU_S = 0.044715, 0.7978845608028654

CONST = {}
_at = 0
for _name, _w in (("ident", P), ("mask", P), ("ones", P), ("band", 4 * P), ("prev", 64), ("first", 64),
                  ("iota", TOPK), ("minus", HEADS), ("eps", 1)):
    CONST[_name] = (_at, _at + _w)
    _at += _w
CONST_W = _at
SMALL = {}
_at = 0
for _name, _w in (("g1", 8), ("fbias", 1), ("wf", KD * HEADS), ("qg", 1), ("kg", 1), ("pscale", 2),
                  ("dskip", 2), ("glub", 2), ("og", 8), ("gluw", 512), ("poolw", 256), ("cre", SB * BCH),
                  ("cim", SB * BCH), ("g2", D)):
    SMALL[_name] = (_at, _at + _w)
    _at += _w
SMALL_W = _at
SMALL_FIRST = SMALL["wf"][1]
TAB = {}
_at = 0
for _name, _w in (("are", SB), ("aim", SB), ("ldt", SB), ("bre", SB * BCH), ("bim", SB * BCH)):
    TAB[_name] = (_at, _at + _w)
    _at += _w
TAB_W = _at
CHUNKS = 20
CH_SSM, CH_POOL, CH_Q, CH_K, CH_V, CH_OUT, CH_ROUTE = 0, 1, 2, 4, 6, 8, 12
CHUNK_W = KD * 256 + 256


MIX = (("normA",), ("normT",), ("u", "uT"), ("pf", "gate", "ln", "cum"), ("bu",), ("qkv0", "scan"),
       ("qkv1", "backA"), ("qkv2", "backB"), ("y", "z", "qkv3"), ("glu", "qkv4", "qkn"), ("qkv5",),
       ("qkT", "v"), ("att0", "max0", "nrm0", "pool"), ("att1", "max1", "nrm1", "mixp", "mixT"),
       ("att2", "max2", "nrm2"), ("att3", "max3", "nrm3"), ("att4", "attT", "sq"), ("merge",), ("out0",),
       ("out1",), ("out2",), ("out3", "x1"), ("h2T", "rp"), ("route0",))
MIX0 = ("normA", "dt", "inverse", "tab0", "tab1", "tab2", "tab3", "tab4",
        "normT", "u", "uT", "pf", "gate", "ln", "cum", ("normA", 1), "qkv0", "qkv1", ("normT", 1),
        "rotate0", "qkv2", "qkv3", "qkn", "rotate1", "qkv4", "qkv5", "bT", "qkT", "v", "rotate2", "bu", "att0",
        ("pf", 1), ("gate", 1), "pool", "max0", "scan", "nrm0", "mixp", "att1", ("u", 1), "backA", "mixT",
        "max1", ("ln", 1), ("qkv0", 1), "backB", "nrm1", ("uT", 1), "att2", "max2", "y", "nrm2", ("qkv1", 1), "z", "att3",
        "max3", "glu", ("cum", 1), "nrm3", ("qkv4", 1), "att4", "attT", "sq", "merge", ("qkv2", 1), ("qkv3", 1),
        ("qkn", 1), "out0", "out1", "out2", ("qkT", 1), "out3", ("qkv5", 1), "x1", ("v", 1), "h2T", "rp",
        "route0")
MIX1 = (("bu",), ("scan",), ("backA",), ("backB",), ("y", "z"), ("glu", "pool", "dt", "inverse"),
        ("att0", "max0", "nrm0"), ("att1", "max1", "nrm1", "mixp", "mixT"), ("att2", "max2", "nrm2", "tab0"),
        ("att3", "max3", "nrm3", "tab1"), ("att4", "attT", "sq", "tab2"), ("merge", "tab3"),
        ("out0",), ("out1",), ("out2",), ("out3", "x1"), ("h2T", "rp"), ("route0",), ("route1",),
        ("route2", "tab4"), ("route3", "tab5"), ("route4", "tab6"), ("route5", "tab7"), ("route6", "bT"),
        ("route7",))
ROUTES = tuple((f"route{h}",) for h in range(1, PH))


def script():
    order = [("mix", s, 0) if type(s) is str else ("mix",) + s for s in MIX0]
    for n in range(STEPS):
        if n == 0:
            rows = [(0, r) for r in ROUTES] + [(1, r) for r in MIX1]
        else:
            rows = [(n + 1, r) for r in MIX + ROUTES] if n + 1 < STEPS else []
        at = 0
        for quad in range(QUADS):
            order.append(("open", n, quad))
            if quad == 0 and n:
                order.append(("mix", "drain", n - 1))
            while at < len(rows) * (quad + 1) // QUADS:
                step, row = rows[at]
                order += [("mix", s, 2 if s[:3] == "tab" or s in ("dt", "inverse", "bT") else step) for s in row]
                at += 1
            order.append(("close", n, quad))
    return order + [("open", n, QUADS), ("close", n, QUADS), ("mix", "drain", STEPS - 1)]


ORDER = script()


def in_slot(n, i):
    return (n == 0 and i < CH_ROUTE) or (n == 1 and i < CH_OUT)


def chunk_order():
    first = {"u": CH_SSM, "pf": CH_POOL, "qkv": CH_Q, "out": CH_OUT, "route": CH_ROUTE}
    order = []
    for kind, a, b in ORDER:
        name = a.rstrip("0123456789") if kind == "mix" else ""
        if name in first:
            order.append((b, first[name] + int(a[len(name):] or 0)))
    return order


USES = chunk_order()
RING = [c for c in USES if not in_slot(*c)]


def uses(n, i):
    return USES.index((n, i)) + 1


def experts_of(n, quad):
    start, end = PICKS * n + GRP * quad, PICKS * n + GRP * quad + GRP
    last = PICKS * STEPS - 1
    if start > last:
        return range(last, last + 1)
    return range(start, min(end, last) if end > last else end)


def added():
    routing, experts = False, {PICKS * STEPS - 2, PICKS * STEPS - 1}
    for kind, a, b in ORDER:
        if kind == "open":
            routing = a == STEPS - 1
        elif kind == "close" and not routing:
            experts.add(experts_of(a, b)[-1])
        elif kind == "mix" and a.startswith("route"):
            routing = True
    return experts


BY_VECTOR = added()


def by_tensor(E):
    return sum(1 for e in range(E) if e not in BY_VECTOR)


def by_vector(E):
    return E - by_tensor(E)


def trunk(nc, x, consts, small, tabs, weights, experts, out):
    ctx = ExitStack()
    with ctx:
        def sb(name, shape, dt=F32):
            return ctx.enter_context(nc.sbuf_tensor(name, shape, dt))

        def sem(name):
            return ctx.enter_context(nc.semaphore(name))

        cst = sb("cst", [P, CONST_W])
        sml = sb("sml", [P, SMALL_W])
        tabp = sb("tabp", [P, TAB_W])
        ring = sb("ring", [P, 2, CHUNK_W])
        slot = sb("slot", [P, SLOTS, 2 * D])
        xs = sb("xs", [P, TILES, D])
        h2 = sb("h2", [P, 2, D])
        hT = sb("hT", [P, KD, P])
        W = [sb(f"work{i}", [P, D]) for i in range(4)]
        rot = sb("rot", [P, 2, SB, P])
        carry = sb("carry", [P, 2, SB])
        base = sb("base", [P, 24, SB])
        bT = sb("bT", [P, 2, 2, P])
        ncim = sb("ncim", [P, SB * BCH])
        ogq = sb("ogq", [P, 2])
        hglub = sb("hglub", [P, 2])
        uT = sb("uT", [P, TILES, 2, P])
        sT = sb("sT", [P, 2, P])
        hT1 = h2[:, 1, :].rearrange("p (a b) -> p a b", a=KD)

        def gl_(n):
            return (ring[:, 1, D:D + 768] if n == 0 else W[2][:, 0:768]).rearrange("p (a b c) -> p a b c", a=3, b=2)

        up = sb("up", [P, TILES, 256])
        qTz = sb("qTz", [P, TILES, PAIRS, 2, P])
        kT = sb("kT", [P, PAIRS, SEQ])
        V = sb("V", [P, TILES, HEADS * DH])
        cT = sb("cT", [P, SEQ])

        def fg_(n):
            where = slot[0:HEADS, 1, D:] if n == 1 else W[2][0:HEADS, :]
            return where[:, 0:5 * P].rearrange("p (a b) -> p a b", a=5)

        def qk_(n):
            return (slot[:, 1, 0:D], slot[:, 1, D:2 * D]) if n == 1 else (W[1][:, :], W[0][:, :])

        def turning(n):
            return ring[:, 1, 0:D] if n == 0 else W[2][:, :]

        def u_at(n):
            return PB[:, 3, 0:256] if n == 1 else PX[:, 0, 0:256]

        def p_at(n):
            return PB[:, 1, 0:256] if n == 1 else PX[:, 1, 0:256]

        def f_at(n):
            return PB[0:HEADS, 1, 256:384] if n == 1 else PX[0:HEADS, 1, 256:384]

        def y_at(n):
            return PB[:, 3, :] if n == 0 else PX[:, 0, :]

        def turned(n, h):
            return PB[:, 0, h % 2 * P:h % 2 * P + P] if n == 0 else PB[:, h % 2, :]

        def hT_(n):
            return hT1 if n == 1 else hT

        def qk_banks(n):
            return (1, PB[:, 0, :], PB[:, 1, :]) if n == 1 else (0, PB[:, 3, :], PX[:, 1, :])

        prob = W[2][:, 0:512].rearrange("p (a b) -> p a b", a=2)
        probT = W[2][:, 512:1024].rearrange("p (a b) -> p a b", a=2)
        att_s = sb("att_s", [P, 3, HEADS])
        rB = sb("rB", [P, 3, P])
        st = sb("st", [P, 8])
        ssqk = sb("ssqk", [P, 3, 16])
        qTs = W[2][:, 0:512].rearrange("p (a b) -> p a b", a=2)
        sc = W[2][:, 512:1024].rearrange("p (a b) -> p a b", a=2)
        cand = W[3][:, 0:768].rearrange("p (a b) -> p a b", a=3)
        sc2 = W[3][:, 768:1024]
        ts = sb("ts", [P, 2, TOPK])
        ti = sb("ti", [P, 2, TOPK], U32)
        tif = sb("tif", [P, 2, TOPK])
        bs = sb("bs", [P, 2, TOPK])
        bj = sb("bj", [P, 3, TOPK], U32)
        bjf = sb("bjf", [P, 2, TOPK])
        ex = sb("ex", [P, 3, TOPK])
        rs = sb("rs", [P, 4])
        idx = sb("idx", [P, 2, PICKS], U32)
        gate = sb("gate", [P, 2, PICKS])
        ge = sb("ge", [P, 7, 2, GRP])
        diag = sb("diag", [P, DIAGS, P])

        acc = ctx.enter_context(nc.psum_tensor("acc", [P, 2, 512], F32))
        PX = ctx.enter_context(nc.psum_tensor("PX", [P, 2, 512], F32))
        PB = ctx.enter_context(nc.psum_tensor("PB", [P, 4, 512], F32))

        names = ["cst_in", "x_in0", "x_in1", "small_in0", "small_in1", "rest_in0", "rest_in1", "ring_in0", "ring_in1", "chunk_used",
                 "zeroed", "tab_in", "inverse_ready", "dt_ready", "doubled", "rot_ready", "sumsq_x", "rms_x", "xn_ready", "xT_psum", "hT_ready", "pf_psum",
                 "uT_ready", "fx_ready", "up_ready", "ln_ready", "c_ready", "bbar_ready", "bT_psum", "bT_ready",
                 "bu_psum", "rot_in_done", "states_ready", "y_psum", "garg_ready", "gtanh_ready", "z_ready",
                 "glu_psum", "sig_ready", "s_ready", "qksq_ready", "qkss_ready",
                 "qkrms_ready", "qkn_ready", "qkT_psum", "qkT_ready", "v_ready", "logits_psum", "nmax_ready",
                 "exp_ready", "prob_ready", "probT_psum", "probT_ready", "pv_psum", "attT_ready",
                 "pool_psum", "pool_ready", "mix_psum", "mixT_ready", "sq_ready", "norm_psum", "norm_rms",
                 "merged_ready", "x1_ready", "sumsq_x1", "rms_x1", "h2_ready", "h2T_psum",
                 "h2T_ready", "qT_psum", "qTs_ready", "sc_ready", "top_ready", "gexp_ready", "routed",
                 "arg_ready", "tanh_ready", "w_ready", "diag_ready", "expert_done", "added", "drained",
                 "out_written", "dve_chain", "act_chain", "pool_chain"]
        S = {name: sem(name) for name in names}
        chunk_in = [sem(f"chunk_in{i}") for i in range(CH_ROUTE)]
        landed = [sem(f"slot_in{i}") for i in range(SLOTS)]

        def c_(name, rows=P):
            a, b = CONST[name]
            return cst[0:rows, a:b]

        def s_(name, rows=P):
            a, b = SMALL[name]
            return sml[0:rows, a:b]

        def t_(name):
            a, b = TAB[name]
            return tabp[:, a:b]


        def b_bar_(l):
            return W[0] if l else ring[:, 1, 0:D]

        ident, ones, eps = c_("ident"), c_("ones"), c_("eps")

        def run(pieces, opened, closed):
            for kind, a, b in ORDER:
                if kind == "open":
                    opened(a, b)
                elif kind == "close":
                    closed(a, b)
                elif a in pieces:
                    pieces[a](b)
                elif a.rstrip("0123456789") in pieces:
                    pieces[a.rstrip("0123456789")](b, int(a.lstrip("abcdefghijklmnopqrstuvwxyz")))

        def rotate(tt, lag, link, scratch, sizes):
            for m in sizes:
                if m == 1:
                    lag(tt(rot[:, 0, :, 0], base[:, 9, :], ones[:, 0:SB], ALU.add))
                    link(tt(rot[:, 1, :, 0], base[:, 11, :], ones[:, 0:SB], ALU.mult))
                er = rot[:, 0, :, m - 1:m].to_broadcast([P, SB, m])
                ei = rot[:, 1, :, m - 1:m].to_broadcast([P, SB, m])
                lo = [rot[:, r, :, 0:m] for r in range(2)]
                hi = [rot[:, r, :, m:2 * m] for r in range(2)]
                t = [scratch[:, i * 512:i * 512 + SB * m].rearrange("p (a b) -> p a b", a=SB) for i in range(2)]
                lag(tt(t[0], lo[1], ei, ALU.mult))
                lag(tt(t[1], lo[1], er, ALU.mult))
                lag(tt(hi[0], lo[0], er, ALU.mult))
                lag(tt(hi[1], lo[0], ei, ALU.mult))
                lag(tt(hi[0], hi[0], t[0], ALU.subtract))
                link(tt(hi[1], hi[1], t[1], ALU.add))

        block = ctx.enter_context(nc.Block())

        @block.sync
        def _(sp):
            sp.dma_start(xs[:, 0, :], x[0]).then_inc(S["x_in0"], 16)
            sp.dma_start(cst[:, :], consts).then_inc(S["cst_in"], 16)
            sp.dma_start(sml[:, 0:SMALL_FIRST], small[0, :, 0:SMALL_FIRST]).then_inc(S["small_in0"], 16)
            sp.dma_start(tabp[:, :], tabs[0]).then_inc(S["tab_in"], 16)
            for i in range(CH_ROUTE):
                sp.dma_start(slot[:, i, :], weights[0, i, :, 0:KD * 256]).then_inc(chunk_in[i], 16)
                if i == 1:
                    sp.dma_start(sml[:, SMALL_FIRST:], small[0, :, SMALL_FIRST:]).then_inc(S["rest_in0"], 16)
                    sp.dma_start(xs[:, 1, :], x[1]).then_inc(S["x_in1"], 16)
            for c, (n, i) in enumerate(RING):
                if n == 1 and RING[c - 1][0] == 0:
                    sp.wait_ge(S["rot_ready"], 1)
                    sp.wait_ge(S["bT_ready"], 1)
                    sp.dma_start(tabp[:, :], tabs[1]).then_inc(S["tab_in"], 16)
                if n == 2 and RING[c - 1][0] == 1:
                    sp.wait_ge(S["routed"], 2 * PH)
                    sp.dma_start(sml[:, 0:SMALL_FIRST], small[1, :, 0:SMALL_FIRST]).then_inc(S["small_in1"], 16)
                    sp.dma_start(sml[:, SMALL_FIRST:], small[1, :, SMALL_FIRST:]).then_inc(S["rest_in1"], 16)
                if c == 1:
                    sp.wait_ge(S["s_ready"], 1)
                if c >= 2:
                    sp.wait_ge(S["chunk_used"], uses(*RING[c - 2]))
                w = CHUNK_W if i >= CH_ROUTE else KD * 256
                sp.dma_start(ring[:, c % 2, 0:w], weights[n // TILES, i, :, 0:w]).then_inc(S[f"ring_in{c % 2}"], 16)
            for n in range(2, STEPS):
                for half in range(2):
                    cols = slice(half * 512, half * 512 + 512)
                    sp.wait_ge(S["drained"], 2 * n + half + 1)
                    sp.dma_start(out[n - 2, :, cols], xs[:, n % 2, cols]).then_inc(S["out_written"], 16)
            sp.wait_ge(S["out_written"], 64)

        @block.gpsimd
        def _(pool):
            chain = [0]

            def link(ins):
                chain[0] += 1
                ins.then_inc(S["pool_chain"], 1)
                pool.wait_ge(S["pool_chain"], chain[0])

            def lag(ins):
                chain[0] += 1
                ins.then_inc(S["pool_chain"], 1)
                if chain[0] > 1:
                    pool.wait_ge(S["pool_chain"], chain[0] - 1)

            def tt(o, a, b, op):
                return pool.tensor_tensor(o, a, b, op)

            def scaled(o, a, number, b, op):
                t = base[:, 16:18, :] if len(a.shape) == 3 else base[:, 3, :]
                link(pool.tensor_scalar(t, a, number, None, op))
                link(tt(o, t, b, ALU.mult))

            pool.memset(qTz[:, :, :, :, :], 0.0)
            pool.memset(cT[:, :], 0.0).then_inc(S["zeroed"], 1)

            def gather(n, quad):
                for E in experts_of(n, quad):
                    e = E - PICKS * n
                    if e % TOPK == 0:
                        pool.wait_ge(S["routed"], PH * n + e // TOPK + 1)
                    if E < SLOTS:
                        pool.wait_ge(S["chunk_used"], max(uses(0, E), uses(1, E) if in_slot(1, E) else 0))
                        pool.wait_ge(S["qkT_ready"], 2)
                    else:
                        if E - SLOTS not in BY_VECTOR:
                            pool.wait_ge(S["expert_done"], by_tensor(E - SLOTS + 1))
                        else:
                            pool.wait_ge(S["added"], by_vector(E - SLOTS + 1))
                    pool.indirect_dma_start(
                        out=slot[:, E % SLOTS, :], out_offset=None, in_=experts,
                        in_offset=bass.IndirectOffsetOnAxis(ap=idx[:, n % 2, e:e + 1], axis=0),
                    ).then_inc(landed[E % SLOTS], 16)

            b = lambda i: base[:, i, :]
            are, aim = t_("are"), t_("aim")
            re, im = base[:, 4:6, :], base[:, 6:8, :]
            ure, uim, t0, t1 = base[:, 8:10, :], base[:, 10:12, :], base[:, 12:14, :], base[:, 14:16, :]
            R, Pr, Pi = b(8), b(9), b(11)

            def exp_start(l):
                pool.wait_ge(S["tab_in"], 16 * (l + 1))
                if l:
                    pool.wait_ge(S["states_ready"], TILES)
                lag(pool.memset(b(5), 0.0))
                lag(pool.memset(b(6), 0.0))
                pool.wait_ge(S["dt_ready"], l + 1)
                lag(tt(b(4), b(0), are, ALU.mult))
                link(tt(b(7), b(0), aim, ALU.mult))
                link(pool.tensor_scalar(base[:, 4:8, :], base[:, 4:8, :], 0.5 ** HALVINGS, None, ALU.mult))
                lag(pool.tensor_scalar(ure, re, 1 / TERMS, 1.0, ALU.mult, ALU.add))
                link(pool.tensor_scalar(uim, im, 1 / TERMS, None, ALU.mult))
                t2, t3 = base[:, 16:18, :], base[:, 18:20, :]
                for k in range(TERMS - 1, 0, -1):
                    lag(tt(t0, re, ure, ALU.mult))
                    lag(tt(t1, im, uim, ALU.mult))
                    lag(tt(t2, re, uim, ALU.mult))
                    lag(tt(t3, im, ure, ALU.mult))
                    lag(tt(t0, t0, t1, ALU.subtract))
                    lag(tt(t2, t2, t3, ALU.add))
                    lag(pool.tensor_scalar(ure, t0, 1 / k, 1.0 if k > 1 else 0.0, ALU.mult, ALU.add))
                    link(pool.tensor_scalar(uim, t2, 1 / k, None, ALU.mult))

            def exp_double(l, times):
                t2 = base[:, 16:18, :]
                for _ in range(times):
                    lag(tt(t1, uim, uim, ALU.mult))
                    lag(pool.tensor_scalar(t0, ure, 2.0, 2.0, ALU.mult, ALU.add))
                    lag(pool.tensor_scalar(t2, ure, 2.0, None, ALU.add))
                    lag(tt(uim, uim, t0, ALU.mult))
                    link(tt(ure, ure, t2, ALU.mult))
                    link(tt(ure, ure, t1, ALU.subtract))

            def coefficients(l):
                pool.tensor_copy(b(10), b(8)).then_inc(S["doubled"], 1)
                link(tt(b(12), R, Pr, ALU.mult))
                link(tt(b(13), R, Pi, ALU.mult))
                link(tt(b(12), b(12), R, ALU.add))
                link(tt(b(13), b(13), Pi, ALU.add))
                link(tt(b(12), b(12), Pr, ALU.add))
                link(tt(b(16), b(12), are, ALU.mult))
                link(tt(b(17), b(13), aim, ALU.mult))
                link(tt(b(18), b(13), are, ALU.mult))
                link(tt(b(19), b(12), aim, ALU.mult))
                link(tt(b(16), b(16), b(17), ALU.add))
                link(tt(b(18), b(18), b(19), ALU.subtract))
                pool.wait_ge(S["inverse_ready"], l + 1)
                link(tt(b(16), b(16), b(23), ALU.mult))
                link(tt(b(17), b(18), b(23), ALU.mult))
                link(pool.tensor_scalar(b(20), R, 1.0, None, ALU.add))

            def b_bar(l):
                if l:
                    pool.wait_ge(S["rms_x1"], TILES)
                cre = b(16).rearrange("p (j f) -> p f j", f=2).unsqueeze(3).to_broadcast([P, 2, 4, BCH])
                cim = b(17).rearrange("p (j f) -> p f j", f=2).unsqueeze(3).to_broadcast([P, 2, 4, BCH])
                v4 = lambda a: a.rearrange("p (f j c) -> p f j c", f=2, j=4)
                q = [b_bar_(l)[:, i * 256:i * 256 + 256] for i in range(4)]
                link(tt(v4(q[0]), v4(t_("bre")), cre, ALU.mult))
                link(tt(v4(q[1]), v4(t_("bim")), cim, ALU.mult))
                link(tt(v4(q[2]), v4(t_("bre")), cim, ALU.mult))
                link(tt(v4(q[3]), v4(t_("bim")), cre, ALU.mult))
                link(tt(q[0], q[0], q[1], ALU.subtract))
                tt(q[2], q[2], q[3], ALU.add).then_inc(S["bbar_ready"], 1)

            def tab(n, part):
                l = n // TILES
                if part == 0:
                    exp_start(l)
                elif part == 1:
                    exp_double(l, HALVINGS // 2)
                elif part == 2:
                    exp_double(l, HALVINGS - HALVINGS // 2)
                elif part == 3:
                    coefficients(l)
                elif part == 4:
                    b_bar(l)
                elif part in (5, 6, 7):
                    if l:
                        rotate(tt, lag, link, W[1], ((1, 2, 4, 8, 16), (32,), (64,))[part - 5])
                    if part == 7 and l:
                        pool.tensor_copy(base[:, 21, :], Pr).then_inc(S["rot_ready"], 1)

            run(dict(tab=tab), gather, lambda n, quad: None)

        @block.scalar
        def _(act):
            chain = [0]

            def link(ins):
                chain[0] += 1
                ins.then_inc(S["act_chain"], 1)
                act.wait_ge(S["act_chain"], chain[0])

            counts = {}

            def told(ins, name):
                counts[name] = counts.get(name, 0) + 1
                ins.then_inc(S[name], 1)
                act.wait_ge(S[name], counts[name])

            def rms(n, ready, count, col, sumsq, done):
                act.wait_ge(S[ready], count)
                told(act.activation(W[1][:, :], xs[:, n % 2, :], ACT.Square, scale=D ** -0.5,
                               accum_out=st[:, col:col + 1]), sumsq)
                if n == 0:
                    act.wait_ge(S["cst_in"], 16)
                told(act.activation(st[:, col + 1:col + 2], st[:, col:col + 1], ACT.Sqrt,
                               bias=eps), done)

            def normA(n):
                if n == TILES:
                    act.wait_ge(S["rot_ready"], 2)
                if n < TILES:
                    rms(n, f"x_in{n}", 16, 0, "sumsq_x", "rms_x")
                else:
                    rms(n, "drained", 2 * (n - 1), 0, "sumsq_x", "rms_x")

            def dt(n):
                l = n // TILES
                act.wait_ge(S["tab_in"], 16 * (l + 1))
                if l:
                    act.wait_ge(S["bT_ready"], 1)
                told(act.activation(base[:, 0, :], t_("ldt"), ACT.Exp), "dt_ready")

            def gate(n):
                act.wait_ge(S["pf_psum"], n + 1)
                told(act.copy(up[:, n % 2, :], p_at(n)), "up_ready")
                told(act.activation(fg_(n)[:, 0, :], f_at(n), ACT.Identity, bias=s_("fbias", HEADS)), "fx_ready")

            def ln(n):
                fg = fg_(n)
                link(act.activation(fg[:, 1, :], fg[:, 0, :], ACT.Abs))
                link(act.activation(fg[:, 2, :], fg[:, 1, :], ACT.Exp, scale=-1.0))
                told(act.activation(fg[:, 3, :], fg[:, 2, :], ACT.Ln, bias=ones[0:HEADS, 0:1]), "ln_ready")

            def turn_b(n):
                l = n // TILES
                act.wait_ge(S["bT_psum"], l + 1)
                told(act.copy(bT[:, :, :, :].rearrange("p a b c -> p (a b c)"), PB[:, 0, :]), "bT_ready")

            def z(n):
                act.wait_ge(S["garg_ready"], n + 1)
                gl = gl_(n)
                told(act.activation(gl[:, 1, :, :], gl[:, 0, :, :], ACT.Tanh, scale=GELU_S), "gtanh_ready")

            def glu(n):
                act.wait_ge(S["glu_psum"], n + 1)
                gl = gl_(n)
                for hf in range(2):
                    ins = act.activation(gl[:, 1, hf, :], y_at(n)[:, 256 + hf * P:256 + hf * P + P], ACT.Tanh,
                                         scale=0.25, bias=hglub[:, hf:hf + 1])
                told(ins, "sig_ready")

            def qkn(n):
                act.wait_ge(S["chunk_used"], uses(n, CH_K + 1))
                if n >= 2:
                    act.wait_ge(S["y_psum"], n + 1)
                b = qk_banks(n)[0]
                told(act.activation(qk_(n)[0], PB[:, b:b + 2, :].rearrange("p a b -> p (a b)"), ACT.Square,
                               scale=DH ** -0.5), "qksq_ready")
                act.wait_ge(S["qkss_ready"], n + 1)
                told(act.activation(ssqk[:, 1, :], ssqk[:, 0, :], ACT.Sqrt, bias=eps), "qkrms_ready")

            def v(n):
                act.wait_ge(S["chunk_used"], uses(n, CH_V + 1))
                told(act.copy(V[:, n % 2, :], PB[:, qk_banks(n)[0] + 2, :]), "v_ready")

            def evict(n, h):
                H = HEADS * n + h
                w = P * (n % 2 + 1)
                act.wait_ge(S["probT_psum"], H + 2 - h % 2 if n == 0 else H + 1)
                if H >= 2:
                    act.wait_ge(S["pv_psum"], H - 1)
                told(act.copy(probT[:, h % 2, 0:w], turned(n, h)[:, 0:w]), "probT_ready")

            def att(n, i):
                w = P * (n % 2 + 1)
                for h in (2 * i - 2, 2 * i - 1):
                    if h >= 0:
                        evict(n, h)
                for h in (2 * i, 2 * i + 1):
                    if h < HEADS:
                        H = HEADS * n + h
                        act.wait_ge(S["nmax_ready"], H + 1)
                        if H >= 2:
                            act.wait_ge(S["probT_psum"], H - 1)
                        told(act.activation(prob[:, h % 2, 0:w], PX[:, h % 2, 0:w], ACT.Exp,
                                            bias=att_s[:, 0, h:h + 1], accum_out=att_s[:, 1, h:h + 1]), "exp_ready")

            def pool_(n):
                act.wait_ge(S["pool_psum"], n + 1)
                told(act.copy(h2[:, n % 2, 512:768], PB[:, 3, 0:256]), "pool_ready")

            def sq(n):
                act.wait_ge(S["attT_ready"], n + 1)
                link(act.activation(W[1][:, 0:512], h2[:, n % 2, 0:512], ACT.Square, scale=(HEADS * DH) ** -0.5))
                act.wait_ge(S["mixT_ready"], n + 1)
                link(act.activation(W[1][:, 512:768], h2[:, n % 2, 768:1024], ACT.Square, scale=1 / 16))
                act.wait_ge(S["s_ready"], n + 1)
                told(act.activation(W[1][:, 768:1024], sT[:, :, :].rearrange("p a b -> p (a b)"), ACT.Square,
                               scale=1 / 64), "sq_ready")

            def merge(n):
                act.wait_ge(S["norm_psum"], n + 1)
                told(act.activation(rB[:, :, :].rearrange("p a b -> p (a b)"), PB[:, 0, 0:3 * P], ACT.Sqrt,
                               bias=eps), "norm_rms")

            def x1_(n):
                rms(n, "x1_ready", n + 1, 2, "sumsq_x1", "rms_x1")

            def h2T(n):
                for half in range(2):
                    act.wait_ge(S["h2T_psum"], 2 * n + half + 1)
                    told(act.copy(hT[:, 4 * half:4 * half + 4, :].rearrange("p a b -> p (a b)"),
                             PB[:, half, :]), "h2T_ready")

            def rp(n, h=0):
                R = PH * n + h
                act.wait_ge(S["qT_psum"], R + 1)
                if R >= 2:
                    act.wait_ge(S["chunk_used"], uses((R - 2) // PH, CH_ROUTE + (R - 2) % PH))
                told(act.copy(qTs[:, h % 2, :], PB[:, 2 + h % 2, 0:256]), "qTs_ready")

            def route(n, h):
                R = PH * n + h
                act.wait_ge(S["chunk_used"], uses(n, CH_ROUTE + h))
                if R >= 2:
                    act.wait_ge(S["routed"], R - 1)
                told(act.copy(sc[:, h % 2, :], PB[:, 2 + h % 2, 256:512]), "sc_ready")
                if h + 1 < PH:
                    rp(n, h + 1)
                act.wait_ge(S["top_ready"], R + 1)
                told(act.activation(bs[:, 1, :], bs[:, 0, :], ACT.Exp, bias=rs[:, 0:1],
                               accum_out=rs[:, 1:2]), "gexp_ready")

            def weigh(n, quad):
                G = QUADS * n + quad
                act.wait_ge(S["arg_ready"], G + 1)
                act.activation(ge[:, 4, G % 2, :], ge[:, 2, G % 2, :], ACT.Tanh,
                               scale=GELU_S).then_inc(S["tanh_ready"], 1)
                act.wait_ge(S["w_ready"], G + 1)
                for i, E in enumerate(experts_of(n, quad)):
                    if E in BY_VECTOR:
                        continue
                    d = by_tensor(E)
                    if d >= DIAGS:
                        act.wait_ge(S["expert_done"], d - DIAGS + 1)
                    act.activation(diag[:, d % DIAGS, :], ident, ACT.Copy,
                                   scale=ge[:, 5, G % 2, i:i + 1]).then_inc(S["diag_ready"], 1)

            run(dict(dt=dt, normA=normA, gate=gate, ln=ln, bT=turn_b, z=z, glu=glu, qkn=qkn, v=v, att=att, pool=pool_, sq=sq,
                     merge=merge, x1=x1_, h2T=h2T, rp=rp, route=route), lambda n, quad: None, weigh)

        @block.vector
        def _(dve):
            chain = [0]

            def link(ins):
                chain[0] += 1
                ins.then_inc(S["dve_chain"], 1)
                dve.wait_ge(S["dve_chain"], chain[0])

            counts = {}

            def told(ins, name):
                counts[name] = counts.get(name, 0) + 1
                ins.then_inc(S[name], 1)
                dve.wait_ge(S[name], counts[name])

            def tt(o, a, b, op):
                return dve.tensor_tensor(o, a, b, op)

            def lag(ins):
                chain[0] += 1
                ins.then_inc(S["dve_chain"], 1)
                if chain[0] > 1:
                    dve.wait_ge(S["dve_chain"], chain[0] - 1)

            def inverse(n):
                dve.wait_ge(S["tab_in"], 16 * (n // TILES + 1))
                lag(tt(base[:, 22, :], t_("are"), t_("are"), ALU.mult))
                link(tt(base[:, 23, :], t_("aim"), t_("aim"), ALU.mult))
                link(tt(base[:, 23, :], base[:, 22, :], base[:, 23, :], ALU.add))
                told(dve.reciprocal(base[:, 23, :], base[:, 23, :]), "inverse_ready")

            def rotate_(n, part):
                if part == 0:
                    dve.wait_ge(S["doubled"], 1)
                    rotate(tt, lag, link, W[3], (1, 2, 4, 8, 16))
                elif part == 1:
                    rotate(tt, lag, link, W[3], (32,))
                else:
                    rotate(tt, lag, link, W[3], (64,))
                    told(dve.tensor_copy(base[:, 21, :], base[:, 9, :]), "rot_ready")

            def normA(n):
                if n < TILES:
                    dve.wait_ge(S[f"x_in{n}"], 16)
                if n == TILES:
                    dve.wait_ge(S["bT_psum"], 2)
                dve.wait_ge(S["rms_x"], n + 1)
                link(dve.reciprocal(st[:, 4:5], st[:, 1:2]))
                told(dve.tensor_scalar(W[0][:, :], xs[:, n % 2, :], st[:, 4:5], None, ALU.mult), "xn_ready")

            def normT(n):
                if n % TILES == 0:
                    dve.wait_ge(S[f"small_in{n // TILES}"], 16)
                for half in range(2):
                    dve.wait_ge(S["xT_psum"], 2 * n + half + 1)
                    g = s_("g1")[:, 4 * half:4 * half + 4].unsqueeze(2).to_broadcast([P, 4, P])
                    told(tt(hT_(n)[:, 4 * half:4 * half + 4, :], PX[:, half, :].rearrange("p (a b) -> p a b", a=4), g,
                       ALU.mult), "hT_ready")

            def u_out(n):
                if n % TILES == 0:
                    dve.wait_ge(S[f"rest_in{n // TILES}"], 16)
                    link(dve.tensor_scalar(ncim[:, :], s_("cim"), -1.0, None, ALU.mult))
                    link(dve.tensor_scalar(ogq[:, :], s_("og")[:, 6:8], 0.25, None, ALU.mult))
                    link(dve.tensor_scalar(hglub[:, :], s_("glub"), 0.5, None, ALU.mult))
                dve.wait_ge(S["chunk_used"], uses(n, CH_SSM))
                told(dve.tensor_copy(uT[:, n % 2, :, :].rearrange("p a b -> p (a b)"), u_at(n)), "uT_ready")

            def cum(n):
                t = n % TILES
                fg = fg_(n)
                if n == 0:
                    dve.wait_ge(S["zeroed"], 1)
                dve.wait_ge(S["ln_ready"], n + 1)
                link(dve.scalar_tensor_tensor(fg[:, 4, :], fg[:, 0, :], 0.0, fg[:, 3, :], ALU.min, ALU.subtract))
                told(dve.tensor_tensor_scan(cT[0:HEADS, t * P:t * P + P], ones[0:HEADS, :], fg[:, 4, :],
                                            cT[0:HEADS, P - 1:P] if t else 0.0, ALU.mult, ALU.add), "c_ready")

            w3 = [w[:, :].rearrange("p (a b) -> p a b", a=SB) for w in W]
            cos_, sin_ = rot[:, 0, :, :], rot[:, 1, :, :]

            def bu(n):
                dve.wait_ge(S["rot_ready"], n // TILES + 1)
                dve.wait_ge(S["bu_psum"], n + 1)
                drive = PB[:, :, :].rearrange("p j (f r t) -> p r (j f) t", f=2, r=2)
                spare = turning(n).rearrange("p (a b) -> p a b", a=SB)
                link(tt(w3[0], drive[:, 0], cos_, ALU.mult))
                link(tt(spare, drive[:, 1], sin_, ALU.mult))
                link(tt(w3[1], drive[:, 1], cos_, ALU.mult))
                told(tt(w3[3], drive[:, 0], sin_, ALU.mult), "rot_in_done")

            def scan(n):
                spare = turning(n).rearrange("p (a b) -> p a b", a=SB)
                link(tt(w3[0], w3[0], spare, ALU.add))
                link(tt(w3[1], w3[1], w3[3], ALU.subtract))
                for r in range(2):
                    for b in range(SB):
                        part = W[r][:, b * P:b * P + P]
                        ins = dve.tensor_tensor_scan(part, base[:, 20, b:b + 1].to_broadcast([P, P]), part,
                                                     carry[:, r, b:b + 1] if n % TILES else 0.0, ALU.mult, ALU.add)
                link(ins)

            def back(n):
                spare = turning(n).rearrange("p (a b) -> p a b", a=SB)
                link(tt(w3[3], w3[0], cos_, ALU.mult))
                link(tt(spare, w3[1], sin_, ALU.mult))
                link(tt(w3[3], w3[3], spare, ALU.subtract))

            def back_im(n):
                link(tt(w3[1], w3[1], cos_, ALU.mult))
                link(tt(w3[0], w3[0], sin_, ALU.mult))
                link(tt(w3[1], w3[1], w3[0], ALU.add))
                link(dve.tensor_copy(carry[:, 0, :], w3[3][:, :, P - 1]))
                told(dve.tensor_copy(carry[:, 1, :], w3[1][:, :, P - 1]), "states_ready")

            def y_(n):
                dve.wait_ge(S["y_psum"], n + 1)
                gl = gl_(n)
                y = gl[:, 2, :, :]
                for hf in range(2):
                    ins = dve.scalar_tensor_tensor(gl[:, 2, hf, :], uT[:, n % 2, hf, :], s_("dskip")[:, hf:hf + 1],
                                                   y_at(n)[:, hf * P:hf * P + P], ALU.mult, ALU.add)
                link(ins)
                link(tt(gl[:, 0, :, :], y, y, ALU.mult))
                link(dve.tensor_scalar(gl[:, 0, :, :], gl[:, 0, :, :], GELU_C, 1.0, ALU.mult, ALU.add))
                told(tt(gl[:, 0, :, :], gl[:, 0, :, :], y, ALU.mult), "garg_ready")

            def z(n):
                gl = gl_(n)
                y = gl[:, 2, :, :]
                dve.wait_ge(S["gtanh_ready"], n + 1)
                told(dve.scalar_tensor_tensor(gl[:, 0, :, :], gl[:, 1, :, :], 1.0, y, ALU.add,
                                         ALU.mult), "z_ready")

            def glu(n):
                gl = gl_(n)
                dve.wait_ge(S["sig_ready"], n + 1)
                told(dve.scalar_tensor_tensor(sT[:, :, :], gl[:, 1, :, :], 1.0, gl[:, 0, :, :], ALU.add,
                                         ALU.mult), "s_ready")

            def qkn(n):
                b = qk_banks(n)[0]
                dve.wait_ge(S["qksq_ready"], n + 1)
                told(dve.tensor_reduce(ssqk[:, 0, :], qk_(n)[0].rearrange("p (a b) -> p a b", a=16), AX.X,
                                  ALU.add), "qkss_ready")
                dve.wait_ge(S["qkrms_ready"], n + 1)
                link(dve.reciprocal(ssqk[:, 2, :], ssqk[:, 1, :]))
                told(tt(qk_(n)[1].rearrange("p (a b) -> p a b", a=16),
                   PB[:, b:b + 2, :].rearrange("p c (a b) -> p (c a) b", a=8),
                   ssqk[:, 2, :].unsqueeze(2).to_broadcast([P, 16, DH]), ALU.mult), "qkn_ready")

            def qkT(n):
                t = n % TILES
                dve.wait_ge(S["qkT_psum"], n + 1)
                qp, kp = (b.rearrange("p (a b) -> p a b", a=PAIRS) for b in qk_banks(n)[1:])
                for o in range(2):
                    r = slice(64 * o, 64 * o + 64)
                    link(dve.tensor_scalar(qTz[r, t, :, o, :], qp[r], s_("qg")[r], DH ** -0.5, ALU.mult, ALU.mult))
                told(dve.tensor_scalar(kT[:, :, t * P:t * P + P], kp, s_("kg"), None, ALU.mult), "qkT_ready")

            def norm_prob(n, h):
                w = P * (n % 2 + 1)
                dve.wait_ge(S["exp_ready"], HEADS * n + h + 1)
                link(dve.reciprocal(att_s[:, 2, h:h + 1], att_s[:, 1, h:h + 1]))
                told(dve.tensor_scalar(prob[:, h % 2, 0:w], prob[:, h % 2, 0:w], att_s[:, 2, h:h + 1], None,
                                  ALU.mult), "prob_ready")

            def biggest(n, i):
                w = P * (n % 2 + 1)
                for h in (2 * i, 2 * i + 1):
                    dve.wait_ge(S["logits_psum"], HEADS * n + h + 1)
                    told(dve.tensor_reduce(att_s[:, 0, h:h + 1], PX[:, h % 2, 0:w], AX.X, ALU.max,
                                      negate=True), "nmax_ready")

            def norm_pair(n, i):
                norm_prob(n, 2 * i)
                norm_prob(n, 2 * i + 1)

            def attT(n):
                dve.wait_ge(S["pv_psum"], HEADS * (n + 1))
                told(dve.tensor_copy(h2[:, n % 2, 0:512], PB[:, 2, :]), "attT_ready")

            def mixT(n):
                dve.wait_ge(S["mix_psum"], n + 1)
                for pr in range(2):
                    ins = dve.tensor_scalar(h2[:, n % 2, 768 + pr * P:768 + pr * P + P],
                                            PB[:, 3, 256 + pr * P:256 + pr * P + P],
                                            s_("pscale")[:, pr:pr + 1], None, ALU.mult)
                told(ins, "mixT_ready")

            def merge(n):
                dve.wait_ge(S["norm_rms"], n + 1)
                link(dve.reciprocal(rB[:, :, :], rB[:, :, :]))
                for k in range(KD):
                    src, g, sec = ((h2[:, n % 2, k * P:k * P + P], s_("og")[:, k:k + 1], 0) if k < 4 else
                                   (h2[:, n % 2, 768 + (k - 4) * P:768 + (k - 3) * P], s_("og")[:, k:k + 1], 1) if k < 6
                                   else (sT[:, k - 6, :], ogq[:, k - 6:k - 5], 2))
                    ins = dve.scalar_tensor_tensor(W[0][:, k * P:k * P + P], src, g, rB[:, sec, :], ALU.mult, ALU.mult)
                    if k % 2:
                        ins.then_inc(S["merged_ready"], 1)
                dve.wait_ge(S["merged_ready"], 4 * (n + 1))

            def x1_(n):
                dve.wait_ge(S["chunk_used"], uses(n, CH_OUT + 3))
                x1 = xs[:, n % 2, :]
                told(tt(x1, x1, PX[:, :, :].rearrange("p a b -> p (a b)"), ALU.add), "x1_ready")
                dve.wait_ge(S["rms_x1"], n + 1)
                link(dve.reciprocal(st[:, 5:6], st[:, 3:4]))
                for half in range(2):
                    c = slice(half * 512, half * 512 + 512)
                    told(dve.scalar_tensor_tensor(h2[:, n % 2, c], x1[:, c], st[:, 5:6], s_("g2")[:, c], ALU.mult,
                                                  ALU.mult), "h2_ready")

            def top16(pairs, after=None):
                step = lag if len(pairs) == 2 else link
                for vals, inds, src, scratch in pairs:
                    step(dve.max(vals[:, 0:8], src))
                for vals, inds, src, scratch in pairs:
                    step(dve.match_replace(scratch, vals[:, 0:8], src, REPLACED))
                for vals, inds, src, scratch in pairs:
                    step(dve.max(vals[:, 8:16], scratch))
                if after:
                    after()
                for vals, inds, src, scratch in pairs:
                    lag(dve.max_index(inds[:, 0:8], vals[:, 0:8], src))
                for vals, inds, src, scratch in pairs:
                    ins = dve.max_index(inds[:, 8:16], vals[:, 8:16], scratch)
                    if len(pairs) == 2:
                        lag(ins)
                    else:
                        link(ins)

            def route(n, h):
                l = n // TILES
                R = PH * n + h
                dve.wait_ge(S["sc_ready"], R + 1)
                top16([(ts[:, i, :], ti[:, i, :], sc[:, h % 2, i * P:i * P + P], sc2[:, i * P:i * P + P])
                       for i in range(2)])
                c3 = lambda i: cand[:, i, :].rearrange("p (a b) -> p a b", a=TOPK)
                rows = lambda a: a.unsqueeze(2).to_broadcast([P, TOPK, TOPK])
                cols = lambda a: a.unsqueeze(1).to_broadcast([P, TOPK, TOPK])
                link(tt(c3(0), rows(ts[:, 0, :]), cols(ts[:, 1, :]), ALU.add))

                def best():
                    told(dve.tensor_scalar(rs[:, 0:1], bs[:, 0, 0:1], -1.0, None, ALU.mult), "top_ready")

                top16([(bs[:, 0, :], bj[:, 0, :], cand[:, 0, :], cand[:, 1, :])], best)
                lag(dve.tensor_copy(tif[:, :, :], ti[:, :, :]))
                lag(dve.tensor_scalar(bj[:, 1, :], bj[:, 0, :], 4, None, ALU.logical_shift_right))
                link(dve.tensor_scalar(bj[:, 2, :], bj[:, 0, :], 15, None, ALU.bitwise_and))
                link(dve.tensor_copy(bjf[:, :, :], bj[:, 1:3, :]))
                both = [P, 2, TOPK, TOPK]
                hot = cand[:, 0:2, :].rearrange("p i (a b) -> p i a b", a=TOPK)
                link(tt(hot, bjf[:, :, :].unsqueeze(3).to_broadcast(both),
                        c_("iota").unsqueeze(1).unsqueeze(1).to_broadcast(both), ALU.is_equal))
                link(tt(hot, hot, tif[:, :, :].unsqueeze(2).to_broadcast(both), ALU.mult))
                link(dve.tensor_reduce(ex[:, 0:2, :], hot, AX.X, ALU.add))
                link(dve.scalar_tensor_tensor(ex[:, 2, :], ex[:, 0, :], float(KEYS), ex[:, 1, :], ALU.mult, ALU.add))
                told(dve.tensor_scalar(idx[:, n % 2, h * TOPK:(h + 1) * TOPK], ex[:, 2, :], float(l * EXPERTS), None,
                                       ALU.add), "routed")
                dve.wait_ge(S["gexp_ready"], R + 1)
                link(dve.reciprocal(rs[:, 2:3], rs[:, 1:2]))
                link(dve.tensor_scalar(gate[:, n % 2, h * TOPK:(h + 1) * TOPK], bs[:, 1, :], rs[:, 2:3], 0.5,
                                       ALU.mult, ALU.mult))

            def drain(n):
                if by_vector(PICKS * (n + 1)):
                    dve.wait_ge(S["added"], by_vector(PICKS * (n + 1)))
                dve.wait_ge(S["expert_done"], by_tensor(PICKS * (n + 1)))
                for half in range(2):
                    x_half = xs[:, n % 2, half * 512:half * 512 + 512]
                    told(tt(x_half, x_half, acc[:, half, :], ALU.add), "drained")

            def ge_(i, n, quad):
                return ge[:, i, (QUADS * n + quad) % 2, 0:len(experts_of(n, quad))]

            def dots(n, quad):
                mine = experts_of(n, quad)
                d, sq, arg, dg = (ge_(i, n, quad) for i in range(4))
                for i, E in enumerate(mine):
                    dve.wait_ge(landed[E % SLOTS], 16 * (E // SLOTS + 1))
                    u = slot[:, E % SLOTS, 0:D]
                    ins = dve.tensor_tensor_reduce(u, u, h2[:, n % 2, :], 1.0, 0.0, ALU.mult, ALU.add, d[:, i:i + 1])
                link(ins)
                lag(tt(dg, d, gate[:, n % 2, mine[0] - PICKS * n:mine[-1] + 1 - PICKS * n], ALU.mult))
                link(tt(sq, d, d, ALU.mult))
                link(dve.tensor_scalar(sq, sq, GELU_C, 1.0, ALU.mult, ALU.add))
                told(tt(arg, sq, d, ALU.mult), "arg_ready")

            def weigh(n, quad):
                G = QUADS * n + quad
                dve.wait_ge(S["tanh_ready"], G + 1)
                w = ge_(5, n, quad)
                if G >= 2:
                    dve.wait_ge(S["diag_ready"], by_tensor(experts_of(*divmod(G - 2, QUADS))[-1] + 1))
                told(dve.scalar_tensor_tensor(w, ge_(4, n, quad), 1.0, ge_(3, n, quad), ALU.add, ALU.mult), "w_ready")
                for i, E in enumerate(experts_of(n, quad)):
                    if E in BY_VECTOR:
                        if by_vector(E):
                            dve.wait_ge(S["added"], by_vector(E))
                        dve.scalar_tensor_tensor(xs[:, n % 2, :], slot[:, E % SLOTS, D:2 * D], w[:, i:i + 1],
                                                 xs[:, n % 2, :], ALU.mult, ALU.add).then_inc(S["added"], 1)

            run(dict(inverse=inverse, rotate=rotate_, normA=normA, normT=normT, uT=u_out, cum=cum,
                     bu=bu, scan=scan, backA=back, backB=back_im, y=y_, z=z, glu=glu, qkn=qkn, qkT=qkT,
                     max=biggest, nrm=norm_pair, attT=attT, mixT=mixT, merge=merge, x1=x1_, route=route,
                     drain=drain), dots, weigh)

        @block.tensor
        def _(pe):
            def chunk(n, i):
                if in_slot(n, i):
                    pe.wait_ge(chunk_in[i], 16)
                    return slot[:, i, :]
                c = RING.index((n, i))
                pe.wait_ge(S[f"ring_in{c % 2}"], 16 * (c // 2 + 1))
                return ring[:, c % 2, :]

            def used(ins):
                ins.then_inc(S["chunk_used"], 1)

            def by_k(c):
                return c[:, 0:KD * 256].rearrange("p (k c) -> p k c", k=KD)

            def normT(n):
                if n == 0:
                    pe.wait_ge(S["cst_in"], 16)
                if n == 1:
                    pe.wait_ge(S["up_ready"], 1)
                    pe.wait_ge(S["fx_ready"], 1)
                pe.wait_ge(S["xn_ready"], n + 1)
                for k in range(KD):
                    ins = pe.transpose(PX[:, k // 4, (k % 4) * P:(k % 4) * P + P], W[0][:, k * P:k * P + P], ident)
                    if k % 4 == 3:
                        ins.then_inc(S["xT_psum"], 1)

            def u(n):
                pe.wait_ge(S["hT_ready"], 2 * n + 2)
                if n == 1:
                    pe.wait_ge(S["mixT_ready"], 1)
                c = by_k(chunk(n, CH_SSM))
                for hf in range(2):
                    for k in range(KD):
                        ins = pe.matmul(u_at(n)[:, hf * P:hf * P + P], c[:, k, hf * P:hf * P + P], hT_(n)[:, k, :],
                                        start=(k == 0), stop=(k == KD - 1))
                used(ins)

            def pf(n):
                if n % TILES == 0:
                    pe.wait_ge(S[f"small_in{n // TILES}"], 16)
                if n == 1:
                    pe.wait_ge(S["rot_in_done"], 1)
                c = by_k(chunk(n, CH_POOL))
                for k in range(KD):
                    ins = pe.matmul(p_at(n), hT_(n)[:, k, :], c[:, k, :], start=(k == 0), stop=(k == KD - 1))
                used(ins)
                wf = s_("wf").rearrange("p (k c) -> p k c", k=KD)
                for k in range(KD):
                    ins = pe.matmul(f_at(n), wf[:, k, :], hT_(n)[:, k, :], start=(k == 0), stop=(k == KD - 1))
                ins.then_inc(S["pf_psum"], 1)

            def turn_b(n):
                pe.wait_ge(S["bbar_ready"], n // TILES + 1)
                if n:
                    pe.wait_ge(S["h2T_ready"], 2 * n)
                else:
                    pe.wait_ge(S["qkn_ready"], 1)
                for hf in range(2):
                    for r in range(2):
                        i = 2 * hf + r
                        ins = pe.transpose(PB[:, 0, i * P:i * P + P],
                                           b_bar_(n // TILES)[:, 512 * r + hf * P:512 * r + hf * P + P], ident)
                ins.then_inc(S["bT_psum"], 1)

            def bu(n):
                pe.wait_ge(S["uT_ready"], n + 1)
                pe.wait_ge(S["bT_ready"], n // TILES + 1)
                if n % TILES == 0:
                    pe.wait_ge(S[f"rest_in{n // TILES}"], 16)
                if n:
                    pe.wait_ge(S["sc_ready"], PH * n)
                else:
                    pe.wait_ge(S["v_ready"], 1)
                    pe.wait_ge(S["qkT_ready"], 1)
                for hf in range(2):
                    for r in range(2):
                        for j in range(4):
                            rows = slice(BCH * j, BCH * j + BCH)
                            ins = pe.matmul(PB[:, j, (2 * hf + r) * P:(2 * hf + r + 1) * P], bT[rows, hf, r, :],
                                            uT[rows, n % 2, hf, :], start=True, stop=True)
                ins.then_inc(S["bu_psum"], 1)

            def qkv(n, i):
                if n >= 2 and i == 0:
                    pe.wait_ge(S["rot_in_done"], n + 1)
                if n == 1 and i == 0:
                    pe.wait_ge(S["up_ready"], 2)
                    pe.wait_ge(S["fx_ready"], 2)
                if n == 1 and i == 2:
                    pe.wait_ge(S["attT_ready"], 1)
                if n == 1 and i == 4:
                    pe.wait_ge(S["sig_ready"], 1)
                bank = qk_banks(n)[0] + i // 2
                c = by_k(chunk(n, CH_Q + i))
                for k in range(KD):
                    ins = pe.matmul(PB[:, bank, (i % 2) * 256:(i % 2) * 256 + 256], hT_(n)[:, k, :], c[:, k, :],
                                    start=(k == 0), stop=(k == KD - 1))
                used(ins)

            def y_(n):
                pe.wait_ge(S["states_ready"], n + 1)
                if n == 0:
                    pe.wait_ge(S["uT_ready"], 2)
                xr, xi = (W[i][:, :].rearrange("p (j f t) -> p j f t", j=4, f=2) for i in (3, 1))
                for hf in range(2):
                    for j in range(4):
                        b = 4 * hf + j
                        o = y_at(n)[BCH * j:BCH * j + BCH, hf * P:hf * P + P]
                        pe.matmul(o, s_("cre")[:, b * BCH:(b + 1) * BCH], xr[:, j, hf, :], start=True, stop=False)
                        ins = pe.matmul(o, ncim[:, b * BCH:(b + 1) * BCH], xi[:, j, hf, :], start=False, stop=True)
                ins.then_inc(S["y_psum"], 1)

            def glu(n):
                pe.wait_ge(S["z_ready"], n + 1)
                gw = s_("gluw").rearrange("p (k c) -> p k c", k=2)
                for hf in range(2):
                    for k in range(2):
                        ins = pe.matmul(y_at(n)[:, 256 + hf * P:256 + hf * P + P], gw[:, k, hf * P:hf * P + P],
                                        gl_(n)[:, 0, k, :], start=(k == 0), stop=(k == 1))
                ins.then_inc(S["glu_psum"], 1)

            def qkT(n):
                pe.wait_ge(S["qkn_ready"], n + 1)
                pe.wait_ge(S["up_ready"], n + 1)
                pe.wait_ge(S["fx_ready"], n + 1)
                if n == 1:
                    pe.wait_ge(S["norm_rms"], 1)
                for i in range(8):
                    o = qk_banks(n)[1 + i // 4][:, (i % 4) * P:(i % 4) * P + P]
                    ins = pe.transpose(o, qk_(n)[1][:, i * P:i * P + P], ident)
                ins.then_inc(S["qkT_psum"], 1)

            def logits(n, h):
                t, w = n % TILES, P * (n % TILES + 1)
                H = HEADS * n + h
                o = PX[:, h % 2, 0:w]
                if h == 0:
                    pe.wait_ge(S["qkT_ready"], n + 1)
                    pe.wait_ge(S["c_ready"], n + 1)
                    if n:
                        pe.wait_ge(S["sig_ready"], n + 1)
                if H >= 2 and h >= 2:
                    pe.wait_ge(S["exp_ready"], H - 1)
                one = ident[:, h:h + 1]
                pe.matmul(o, qTz[:, t, h // 2, h % 2, :], kT[:, h // 2, 0:w], start=True, stop=False)
                pe.matmul(o, c_("minus")[:, h:h + 1].to_broadcast([P, P]), cT[:, 0:w], start=False, stop=False)
                pe.matmul(o, cT[:, t * P:t * P + P], one.to_broadcast([P, w]), start=False, stop=False)
                pe.matmul(PX[:, h % 2, t * P:t * P + P], ident, c_("mask"), start=False,
                          stop=True).then_inc(S["logits_psum"], 1)

            def turn(n, h):
                H = HEADS * n + h
                if h == 0:
                    pe.wait_ge(S["rot_in_done"], n + 1)
                pe.wait_ge(S["prob_ready"], H + 1)
                if h >= 2:
                    pe.wait_ge(S["probT_ready"], H - h % 2 if n == 0 else H - 1)
                for b in range(n % TILES + 1):
                    ins = pe.transpose(turned(n, h)[:, b * P:b * P + P], prob[:, h % 2, b * P:b * P + P], ident)
                ins.then_inc(S["probT_psum"], 1)

            def pv(n, h):
                H = HEADS * n + h
                t = n % TILES
                if h == 0:
                    pe.wait_ge(S["v_ready"], n + 1)
                pe.wait_ge(S["probT_ready"], H + 1)
                o = PB[DH * (h % 2):DH * (h % 2) + DH, 2, (h // 2) * P:(h // 2) * P + P]
                for b in range(t + 1):
                    ins = pe.matmul(o, V[:, b, h * DH:(h + 1) * DH], probT[:, h % 2, b * P:b * P + P],
                                    start=(b == 0), stop=(b == t))
                ins.then_inc(S["pv_psum"], 1)

            def att(n, i):
                before = [h for h in (2 * i - 2, 2 * i - 1) if h >= 0]
                for h in before:
                    turn(n, h)
                for h in (2 * i, 2 * i + 1):
                    if h < HEADS:
                        logits(n, h)
                for h in before:
                    pv(n, h)

            def pool_(n):
                t = n % TILES
                pe.wait_ge(S["up_ready"], n + 1)
                pe.wait_ge(S["qkT_ready"], n + 1)
                pe.wait_ge(S["rot_in_done"], n + 1)
                band = c_("band").rearrange("p (g t) -> p g t", g=4)
                edge = c_("prev" if t else "first").rearrange("p (g t) -> p g t", g=4)
                for g in range(4):
                    o = PB[64 * (g % 2):64 * (g % 2) + 64, 3, (g // 2) * P:(g // 2) * P + P]
                    pe.matmul(o, up[:, t, g * 64:g * 64 + 64], band[:, g, :], start=True, stop=False)
                    ins = pe.matmul(o[:, 0:16], up[:, 0, g * 64:g * 64 + 64], edge[:, g, :], start=False, stop=True)
                ins.then_inc(S["pool_psum"], 1)

            def mixp(n):
                pe.wait_ge(S["pool_ready"], n + 1)
                for pr in range(2):
                    ins = pe.matmul(PB[:, 3, 256 + pr * P:256 + pr * P + P], s_("poolw")[:, pr * P:pr * P + P],
                                    h2[:, n % 2, 512 + pr * P:512 + pr * P + P], start=True, stop=True)
                ins.then_inc(S["mix_psum"], 1)

            def merge(n):
                pe.wait_ge(S["sq_ready"], n + 1)
                for sec, ks in enumerate((range(0, 4), range(4, 6), range(6, 8))):
                    for k in ks:
                        ins = pe.matmul(PB[:, 0, sec * P:sec * P + P], ones, W[1][:, k * P:k * P + P],
                                        start=(k == ks[0]), stop=(k == ks[-1]))
                ins.then_inc(S["norm_psum"], 1)

            def out_(n, i):
                pe.wait_ge(S["merged_ready"], 4 * n + i + 1)
                c = chunk(n, CH_OUT + i)
                for k in (2 * i, 2 * i + 1):
                    for half in range(2):
                        ins = pe.matmul(PX[:, half, :], W[0][:, k * P:k * P + P],
                                        c[:, (k % 2) * D + half * 512:(k % 2) * D + half * 512 + 512],
                                        start=(k == 0), stop=(k == KD - 1))
                used(ins)

            def h2T(n):
                if n == 0:
                    pe.wait_ge(S["qkT_ready"], 2)
                for k in range(KD):
                    if k % 4 == 0:
                        pe.wait_ge(S["h2_ready"], 2 * n + k // 4 + 1)
                    ins = pe.transpose(PB[:, k // 4, (k % 4) * P:(k % 4) * P + P], h2[:, n % 2, k * P:k * P + P], ident)
                    if k % 4 == 3:
                        ins.then_inc(S["h2T_psum"], 1)

            def rp(n, h=0):
                R = PH * n + h
                if h == 0:
                    pe.wait_ge(S["h2T_ready"], 2 * n + 2)
                elif R == 1:
                    pe.wait_ge(S["v_ready"], 2)
                else:
                    pe.wait_ge(S["sc_ready"], R - 1)
                c = by_k(chunk(n, CH_ROUTE + h))
                for i in range(2):
                    for k in range(KD):
                        ins = pe.matmul(PB[:, 2 + h % 2, i * P:i * P + P], c[:, k, i * P:i * P + P], hT[:, k, :],
                                        start=(k == 0), stop=(k == KD - 1))
                ins.then_inc(S["qT_psum"], 1)

            def route(n, h):
                pe.wait_ge(S["qTs_ready"], PH * n + h + 1)
                raw = chunk(n, CH_ROUTE + h)
                for i in range(2):
                    ins = pe.matmul(PB[:, 2 + h % 2, 256 + i * P:256 + i * P + P], qTs[:, h % 2, i * P:i * P + P],
                                    raw[:, KD * 256 + i * P:KD * 256 + i * P + P], start=True, stop=True)
                used(ins)
                if h + 1 < PH:
                    rp(n, h + 1)

            waiting = []

            def add_last():
                if not waiting:
                    return
                n, quad = waiting.pop()
                if quad == 0 and n:
                    pe.wait_ge(S["drained"], 2 * n)
                for E in experts_of(n, quad):
                    if E in BY_VECTOR:
                        continue
                    d = by_tensor(E)
                    pe.wait_ge(S["diag_ready"], d + 1)
                    for half in range(2):
                        ins = pe.matmul(acc[:, half, :], diag[:, d % DIAGS, :],
                                        slot[:, E % SLOTS, D + half * 512:D + half * 512 + 512],
                                        start=(E % PICKS == 0), stop=(d + 1 == by_tensor(PICKS * (n + 1))),
                                        skip_group_check=True)
                    ins.then_inc(S["expert_done"], 1)

            def close(n, quad):
                add_last()
                waiting.append((n, quad))

            run(dict(normT=normT, u=u, pf=pf, bT=turn_b, bu=bu, qkv=qkv, y=y_, glu=glu, qkT=qkT, att=att, pool=pool_,
                     mixp=mixp, merge=merge, out=out_, h2T=h2T, rp=rp, route=route), lambda n, quad: None, close)
            add_last()


def const_pack():
    c = np.zeros((P, CONST_W), np.float32)

    def put(name, a):
        c[:, CONST[name][0]:CONST[name][1]] = a

    s, t = np.arange(P)[:, None], np.arange(P)[None, :]
    put("ident", np.eye(P))
    put("mask", np.where(t <= s, 0.0, NEG))
    put("ones", 1.0)
    band, prev, first = np.zeros((P, 4, P)), np.zeros((P, 4, 16)), np.zeros((P, 4, 16))
    for g, w in enumerate(WINDOWS):
        inside = (s <= t) & (s > t - w)
        band[:, g] = inside / w - (s == t)
        prev[:, g] = ((s - P > t - w) / w)[:, :16]
        first[:, g] = (inside / np.minimum(t + 1, w) - inside / w)[:, :16]
    put("band", band.reshape(P, -1))
    put("prev", prev.reshape(P, -1))
    put("first", first.reshape(P, -1))
    put("iota", np.arange(TOPK)[None, :])
    put("minus", -np.eye(P, HEADS))
    put("eps", EPS)
    return c


def small_pack(i):
    L = DEPTH
    o = np.zeros((L, P, SMALL_W), np.float32)
    tab = np.zeros((L, P, TAB_W), np.float32)

    def put(name, a):
        to, (c0, c1) = (tab, TAB[name]) if name in TAB else (o, SMALL[name])
        to[:, :a.shape[1], c0:c1] = a

    def cols(a, k):
        return a.reshape(L, k, P).transpose(0, 2, 1)

    def states(a):
        return a.reshape(L, 2, 4, 2, STATE).transpose(0, 3, 4, 2, 1).reshape(L, P, SB)

    def block_diagonal(a, inner):
        _, b, g, r, c = a.shape
        z = np.zeros((L, g, r, b, g, c), np.float32)
        for gi in range(g):
            z[:, gi, :, :, gi, :] = a[:, :, gi].transpose(0, 2, 1, 3)
        return z.reshape(L, g * r, b * g * c)

    put("g1", cols(i["norm1_g"], 8))
    put("qg", np.concatenate([i["q_gain"]] * 2, 1)[:, :, None])
    put("kg", np.concatenate([i["k_gain"]] * 2, 1)[:, :, None])
    put("pscale", cols(i["pool_scale"], 2))
    put("dskip", cols(i["ssm_d"], 2))
    put("glub", cols(i["glu_b"], 2))
    put("og", cols(i["out_norm_g"], 8))
    put("fbias", i["f_bias"][:, :, None])
    put("are", states(i["ssm_a_re"]))
    put("aim", states(i["ssm_a_im"]))
    put("ldt", states(np.repeat(i["ssm_log_dt"][:, :, None], STATE, 2)))
    f0 = 3 * HEADS * DH
    put("wf", i["w_in"][:, :, f0:f0 + HEADS].reshape(L, KD, P, HEADS).transpose(0, 2, 1, 3).reshape(L, P, -1))
    put("gluw", i["glu_w"].reshape(L, 2, P, 256).transpose(0, 2, 1, 3).reshape(L, P, -1))
    put("poolw", block_diagonal(i["pool_w"].reshape(L, 2, 2, 64, 64), 64))
    for name, key in (("bre", "ssm_b_re"), ("bim", "ssm_b_im")):
        put(name, block_diagonal(i[key].reshape(L, SB, 2, STATE, GCH), GCH))
    for name, key in (("cre", "ssm_c_re"), ("cim", "ssm_c_im")):
        put(name, block_diagonal(i[key].transpose(0, 1, 3, 2).reshape(L, SB, 2, STATE, GCH), GCH))
    put("g2", np.broadcast_to(i["norm2_g"][:, None, :], (L, P, D)))
    return o, tab


def weight_pack(i):
    L = DEPTH
    o = np.zeros((L, CHUNKS, P, CHUNK_W), np.float32)

    def by_k(w):
        return w.reshape(L, KD, P, 256).transpose(0, 2, 1, 3).reshape(L, P, KD * 256)

    w_in = i["w_in"]
    f1 = 3 * HEADS * DH + HEADS
    o[:, CH_SSM, :, :KD * 256] = by_k(w_in[:, :, f1 + 256:f1 + 512])
    o[:, CH_POOL, :, :KD * 256] = by_k(w_in[:, :, f1:f1 + 256])
    for c in range(6):
        o[:, CH_Q + c, :, :KD * 256] = by_k(w_in[:, :, c * 256:c * 256 + 256])
    for c in range(4):
        o[:, CH_OUT + c, :, :2 * D] = (i["w_out"][:, c * 256:c * 256 + 256].reshape(L, 2, P, D)
                                       .transpose(0, 2, 1, 3).reshape(L, P, 2 * D))
    for h in range(PH):
        o[:, CH_ROUTE + h, :, :KD * 256] = by_k(i["peer_wq"][:, :, h * 256:h * 256 + 256])
        o[:, CH_ROUTE + h, :, KD * 256:] = i["peer_keys"][:, h].transpose(0, 3, 1, 2).reshape(L, P, 256)
    return o


def kernel(**inputs):
    import concourse.bacc as _bacc
    from concourse.bass_utils import run_bass_kernel_spmd as _run

    i = {k: np.asarray(v) for k, v in inputs.items()}
    small, tabs = small_pack(i)
    arrays = {
        "x": np.ascontiguousarray(i["x"].reshape(TILES, P, D)),
        "consts": const_pack(),
        "small": small,
        "tabs": tabs,
        "weights": weight_pack(i),
        "experts": np.concatenate([i["peer_u"], i["peer_v"]], 2).reshape(DEPTH * EXPERTS, 2 * D),
    }
    nc = _bacc.Bacc("TRN2", target_bir_lowering=False, num_devices=1)
    args = [nc.dram_tensor(k, a.shape, F32, kind="ExternalInput").ap() for k, a in arrays.items()]
    out = nc.dram_tensor("out", (TILES, P, D), F32, kind="ExternalOutput").ap()
    trunk(nc, *args, out)
    r = _run(nc, [arrays], core_ids=[0])
    return r.results[0]["out"].reshape(1, SEQ, D)
```
